# Optimizing a Trainium2 kernel written in Bass

```python
import numpy as np
import jax
import jax.numpy as jnp
from jax import lax

D_MODEL = 2048
BATCH = 1
SEQ = 256
DEPTH = 1
DEC_BATCH = 8
DEC_SEQ = 8
PAST_LEN = 256
PAGE_SIZE = 128

HEAD_DIM = 128
NSA_HEADS = 8
NSA_KV_HEADS = 2
NSA_GROUP = NSA_HEADS // NSA_KV_HEADS
CMP_LEN = 32
CMP_STRIDE = 16
SEL_BLOCK = 64
SEL_TOP_N = 16
WINDOW = 512
FORCE_BONUS = 1.0e4
MOBA_HEADS = 4
MOBA_BLOCK = 256
MOBA_TOP_K = 3
MEM_HEADS = 4
N_MEM = 256
NSA_Q_BLOCK = 64
MOBA_Q_BLOCK = 32
NSA_WIDTH = NSA_HEADS * HEAD_DIM
NSA_KV_WIDTH = NSA_KV_HEADS * HEAD_DIM
MOBA_WIDTH = MOBA_HEADS * HEAD_DIM
MEM_WIDTH = MEM_HEADS * HEAD_DIM
N_BRANCH = 3
IN_SPLITS = (NSA_WIDTH, 2 * NSA_KV_WIDTH, 2 * NSA_KV_WIDTH, 2 * NSA_KV_WIDTH, 3 * NSA_HEADS, NSA_WIDTH,
             MOBA_WIDTH, 2 * MOBA_WIDTH, MOBA_WIDTH, MEM_WIDTH, MEM_WIDTH, N_BRANCH * D_MODEL)
IN_WIDTH = sum(IN_SPLITS)
RMS_EPS = 1e-6
NEG_INF = -1e30

kernel_name = 'hybrid_nsa_moba_memory_step'

def alibi_slopes(n_heads):
    return jnp.asarray(2.0 ** (-8.0 * np.arange(1, n_heads + 1) / n_heads), dtype=jnp.float32)

def rmsnorm(x, g):
    x32 = x.astype(jnp.float32)
    inv = lax.rsqrt(jnp.mean(x32 * x32, axis=-1, keepdims=True) + RMS_EPS)
    return (x32 * inv * g.astype(jnp.float32)).astype(x.dtype)

def masked_softmax(s, mask):
    s = jnp.where(mask, s, NEG_INF)
    e = jnp.where(mask, jnp.exp(s - jnp.max(s, axis=-1, keepdims=True)), 0.0)
    d = jnp.sum(e, axis=-1, keepdims=True)
    return e / jnp.where(d > 0, d, 1.0)

def in_projection(x, norm_g, w_in):
    h = rmsnorm(x, norm_g) @ w_in
    return jnp.split(h, [int(c) for c in np.cumsum(IN_SPLITS)[:-1]], axis=-1)

def gather_pages(pool, page_table):
    rows = pool[page_table]
    return rows.reshape((page_table.shape[0], -1) + pool.shape[2:])

def nsa_heads(a):
    b, t = a.shape[:2]
    return a.reshape(b, t, NSA_KV_HEADS, NSA_GROUP, -1).transpose(0, 2, 3, 1, 4)

def nsa_rows(o):
    b, g, r, t, d = o.shape
    return o.transpose(0, 3, 1, 2, 4).reshape(b, t, g * r * d)

def split_heads(a, n_heads):
    b, t = a.shape[:2]
    return a.reshape(b, t, n_heads, HEAD_DIM).transpose(0, 2, 1, 3)

def head_rows(o):
    b, h, t, d = o.shape
    return o.transpose(0, 2, 1, 3).reshape(b, t, h * d)

def compress_tokens(kv, phi_pos, phi_w1, phi_w2):
    b, seq_len = kv.shape[:2]
    n_sub = CMP_LEN // CMP_STRIDE
    n_half = seq_len // CMP_STRIDE
    n_cmp = n_half - n_sub + 1
    sub = kv[:, :n_half * CMP_STRIDE].reshape(b, n_half, CMP_STRIDE, 2, NSA_KV_HEADS, HEAD_DIM)
    pos = phi_pos.reshape(2, n_sub, CMP_STRIDE, HEAD_DIM)
    w1 = phi_w1.reshape(2, n_sub, CMP_STRIDE, HEAD_DIM, HEAD_DIM)
    hid = None
    for m in range(n_sub):
        part = jnp.einsum('bnscgd,csdh->bncgh', sub + pos[:, m].transpose(1, 0, 2)[:, :, None, :], w1[:, m])
        part = part[:, m:m + n_cmp]
        hid = part if hid is None else hid + part
    out = jnp.einsum('bncgh,che->bncge', jax.nn.silu(hid), phi_w2)
    ends = jnp.asarray(np.arange(n_cmp) * CMP_STRIDE + CMP_LEN - 1, dtype=jnp.int32)
    return out[:, :, 0].transpose(0, 2, 1, 3), out[:, :, 1].transpose(0, 2, 1, 3), ends

def to_blocks(kv, block):
    b, seq_len, _, h, _ = kv.shape
    nb = -(-seq_len // block)
    kv = jnp.pad(kv, ((0, 0), (0, nb * block - seq_len), (0, 0), (0, 0), (0, 0)))
    kv = kv.reshape(b, nb, block, 2, h, HEAD_DIM).transpose(3, 0, 4, 1, 2, 5)
    return kv[0], kv[1]

def block_means(kb):
    return jnp.mean(kb.astype(jnp.float32), axis=3).astype(kb.dtype)

def nsa_attend(q, gates, q_pos, kc, vc, kc_end, ks, vs, kw, vw, kw_pos, slopes):
    scale = HEAD_DIM ** -0.5
    b, g, r, tq, _ = q.shape
    s = jnp.einsum('bgrtd,bgnd->bgrtn', q, kc).astype(jnp.float32) * scale
    p_cmp = masked_softmax(s, kc_end[None, :] <= q_pos[:, None])
    o_cmp = jnp.einsum('bgrtn,bgnd->bgrtd', p_cmp.astype(vc.dtype), vc)
    n_cmp, n_sel = kc.shape[2], ks.shape[2]
    c_start = np.arange(n_cmp)[:, None] * CMP_STRIDE
    s_start = np.arange(n_sel)[None, :] * SEL_BLOCK
    cover = jnp.asarray(((c_start < s_start + SEL_BLOCK) & (c_start + CMP_LEN > s_start)).astype(np.float32))
    imp = jnp.einsum('bgrtn,ns->bgts', p_cmp, cover)
    blk = jnp.arange(n_sel, dtype=jnp.int32)[None, :]
    cur = (q_pos // SEL_BLOCK)[:, None]
    forced = (blk == 0) | (blk == cur) | (blk == cur - 1)
    allowed = blk * SEL_BLOCK <= q_pos[:, None]
    score = jnp.where(allowed, imp + FORCE_BONUS * forced, NEG_INF)
    n_top = min(SEL_TOP_N, n_sel)
    _, idx = lax.top_k(score, n_top)
    bi = jnp.arange(b)[:, None, None, None]
    gi = jnp.arange(g)[None, :, None, None]
    m_keys = n_top * SEL_BLOCK
    k_sel = ks[bi, gi, idx].reshape(b, g, tq, m_keys, HEAD_DIM)
    v_sel = vs[bi, gi, idx].reshape(b, g, tq, m_keys, HEAD_DIM)
    dist = q_pos[:, None, None] - (idx[..., None] * SEL_BLOCK + jnp.arange(SEL_BLOCK, dtype=jnp.int32))
    dist = dist.reshape(b, g, 1, tq, m_keys)
    s = jnp.einsum('bgrtd,bgtmd->bgrtm', q, k_sel).astype(jnp.float32) * scale
    s = s - slopes[None, :, :, None, None] * dist
    p = masked_softmax(s, dist >= 0)
    o_sel = jnp.einsum('bgrtm,bgtmd->bgrtd', p.astype(v_sel.dtype), v_sel)
    dist_w = q_pos[:, None] - kw_pos[None, :]
    s = jnp.einsum('bgrtd,bgld->bgrtl', q, kw).astype(jnp.float32) * scale
    s = s - slopes[None, :, :, None, None] * dist_w
    p = masked_softmax(s, (dist_w >= 0) & (dist_w < WINDOW) & (kw_pos[None, :] >= 0))
    o_win = jnp.einsum('bgrtl,bgld->bgrtd', p.astype(vw.dtype), vw)
    return gates[..., 0:1] * o_cmp + gates[..., 1:2] * o_sel + gates[..., 2:3] * o_win

def nsa_prompt(q, gates, kc, vc, kc_end, ks, vs, kw, vw, slopes):
    b, g, r, t, dh = q.shape
    nq = t // NSA_Q_BLOCK
    span = WINDOW + NSA_Q_BLOCK

    def to_chunks(a):
        return jnp.moveaxis(a.reshape(b, g, r, nq, NSA_Q_BLOCK, a.shape[-1]), 3, 0)

    kw_pad = jnp.pad(kw, ((0, 0), (0, 0), (WINDOW, 0), (0, 0)))
    vw_pad = jnp.pad(vw, ((0, 0), (0, 0), (WINDOW, 0), (0, 0)))
    starts = jnp.arange(nq, dtype=jnp.int32) * NSA_Q_BLOCK

    def one(args):
        q_c, g_c, s0 = args
        q_pos = s0 + jnp.arange(NSA_Q_BLOCK, dtype=jnp.int32)
        kw_c = lax.dynamic_slice_in_dim(kw_pad, s0, span, axis=2)
        vw_c = lax.dynamic_slice_in_dim(vw_pad, s0, span, axis=2)
        kw_pos = s0 - WINDOW + jnp.arange(span, dtype=jnp.int32)
        return nsa_attend(q_c, g_c, q_pos, kc, vc, kc_end, ks, vs, kw_c, vw_c, kw_pos, slopes)

    out = lax.map(one, (to_chunks(q), to_chunks(gates), starts))
    return jnp.moveaxis(out, 0, 3).reshape(b, g, r, t, dh)

def moba_attend(q, q_pos, kb, vb, kmean, slopes):
    scale = HEAD_DIM ** -0.5
    b, h, tq, _ = q.shape
    nb = kb.shape[2]
    cur = q_pos // MOBA_BLOCK
    gate = jnp.einsum('bhtd,bhnd->bhtn', q, kmean).astype(jnp.float32)
    past = jnp.arange(nb, dtype=jnp.int32)[None, :] < cur[:, None]
    gate = jnp.where(past, gate, NEG_INF)
    own = jnp.broadcast_to(cur, (b, h, tq))[..., None]
    n_top = min(MOBA_TOP_K, nb - 1)
    if n_top > 0:
        top_val, top_idx = lax.top_k(gate, n_top)
        idx = jnp.concatenate([top_idx.astype(jnp.int32), own], axis=-1)
        slot_ok = jnp.concatenate([top_val > 0.5 * NEG_INF, jnp.ones(own.shape, dtype=bool)], axis=-1)
    else:
        idx = own
        slot_ok = jnp.ones(own.shape, dtype=bool)
    n_slot = idx.shape[-1]
    bi = jnp.arange(b)[:, None, None, None]
    hi = jnp.arange(h)[None, :, None, None]
    m_keys = n_slot * MOBA_BLOCK
    k_g = kb[bi, hi, idx].reshape(b, h, tq, m_keys, HEAD_DIM)
    v_g = vb[bi, hi, idx].reshape(b, h, tq, m_keys, HEAD_DIM)
    dist = q_pos[:, None, None] - (idx[..., None] * MOBA_BLOCK + jnp.arange(MOBA_BLOCK, dtype=jnp.int32))
    mask = (slot_ok[..., None] & (dist >= 0)).reshape(b, h, tq, m_keys)
    dist = dist.reshape(b, h, tq, m_keys)
    s = jnp.einsum('bhtd,bhtmd->bhtm', q, k_g).astype(jnp.float32) * scale
    s = s - slopes[None, :, None, None] * dist
    p = masked_softmax(s, mask)
    return jnp.einsum('bhtm,bhtmd->bhtd', p.astype(v_g.dtype), v_g)

def moba_prompt(q, kb, vb, kmean, slopes):
    b, h, t, dh = q.shape
    nq = t // MOBA_Q_BLOCK
    q_c = jnp.moveaxis(q.reshape(b, h, nq, MOBA_Q_BLOCK, dh), 2, 0)
    starts = jnp.arange(nq, dtype=jnp.int32) * MOBA_Q_BLOCK

    def one(args):
        qc, s0 = args
        return moba_attend(qc, s0 + jnp.arange(MOBA_Q_BLOCK, dtype=jnp.int32), kb, vb, kmean, slopes)

    out = lax.map(one, (q_c, starts))
    return jnp.moveaxis(out, 0, 2).reshape(b, h, t, dh)

def cross_attend(q, k, v):
    s = jnp.einsum('bhtd,bhmd->bhtm', q, k).astype(jnp.float32) * (HEAD_DIM ** -0.5)
    p = jax.nn.softmax(s, axis=-1)
    return jnp.einsum('bhtm,bhmd->bhtd', p.astype(v.dtype), v)

def merge_branches(x, o_nsa, z_nsa, o_moba, z_moba, o_mem, z_mem, gate_logits, w_br_nsa, w_br_moba, w_br_mem, w_out):
    branches = jnp.stack([(o_nsa * jax.nn.silu(z_nsa)) @ w_br_nsa,
                          (o_moba * jax.nn.silu(z_moba)) @ w_br_moba,
                          (o_mem * jax.nn.silu(z_mem)) @ w_br_mem], axis=-2)
    gates = jax.nn.sigmoid(gate_logits.reshape(gate_logits.shape[:-1] + (N_BRANCH, D_MODEL)))
    return x + jnp.sum(gates * branches, axis=-2) @ w_out

def prompt_layer(x, mem, norm_g, w_in, phi_pos, phi_w1, phi_w2, mem_norm_g, w_mem_kv,
                 w_br_nsa, w_br_moba, w_br_mem, w_out):
    b, t, _ = x.shape
    (q_nsa, cmp_kv, sel_kv, win_kv, g_nsa, z_nsa, q_moba, moba_kv, z_moba,
     q_mem, z_mem, g_merge) = in_projection(x, norm_g, w_in)
    cmp_kv = cmp_kv.reshape(b, t, 2, NSA_KV_HEADS, HEAD_DIM)
    sel_kv = sel_kv.reshape(b, t, 2, NSA_KV_HEADS, HEAD_DIM)
    win_kv = win_kv.reshape(b, t, 2, NSA_KV_HEADS, HEAD_DIM)
    moba_kv = moba_kv.reshape(b, t, 2, MOBA_HEADS, HEAD_DIM)
    nsa_slopes = alibi_slopes(NSA_HEADS).reshape(NSA_KV_HEADS, NSA_GROUP)
    kc, vc, kc_end = compress_tokens(cmp_kv, phi_pos, phi_w1, phi_w2)
    ks, vs = to_blocks(sel_kv, SEL_BLOCK)
    o_nsa = nsa_prompt(nsa_heads(q_nsa), jax.nn.sigmoid(nsa_heads(g_nsa)), kc, vc, kc_end, ks, vs,
                       win_kv[:, :, 0].transpose(0, 2, 1, 3), win_kv[:, :, 1].transpose(0, 2, 1, 3), nsa_slopes)
    kb, vb = to_blocks(moba_kv, MOBA_BLOCK)
    o_moba = moba_prompt(split_heads(q_moba, MOBA_HEADS), kb, vb, block_means(kb), alibi_slopes(MOBA_HEADS))
    mem_kv = (rmsnorm(mem, mem_norm_g) @ w_mem_kv).reshape(b, mem.shape[1], 2, MEM_HEADS, HEAD_DIM)
    o_mem = cross_attend(split_heads(q_mem, MEM_HEADS), mem_kv[:, :, 0].transpose(0, 2, 1, 3),
                         mem_kv[:, :, 1].transpose(0, 2, 1, 3))
    y = merge_branches(x, nsa_rows(o_nsa), z_nsa, head_rows(o_moba), z_moba, head_rows(o_mem), z_mem, g_merge,
                       w_br_nsa, w_br_moba, w_br_mem, w_out)
    keep = min(WINDOW, t)
    return y, (cmp_kv, sel_kv, moba_kv, win_kv[:, t - keep:], mem_kv)

def sample_layer(x, cache_cmp, cache_sel, cache_moba, cache_win, cache_mem, page_table, norm_g, w_in,
                 phi_pos, phi_w1, phi_w2, w_br_nsa, w_br_moba, w_br_mem, w_out):
    b, t, _ = x.shape
    past = page_table.shape[1] * cache_cmp.shape[1]
    (q_nsa, cmp_kv, sel_kv, win_kv, g_nsa, z_nsa, q_moba, moba_kv, z_moba,
     q_mem, z_mem, g_merge) = in_projection(x, norm_g, w_in)
    cmp_kv = cmp_kv.reshape(b, t, 2, NSA_KV_HEADS, HEAD_DIM)
    sel_kv = sel_kv.reshape(b, t, 2, NSA_KV_HEADS, HEAD_DIM)
    win_kv = win_kv.reshape(b, t, 2, NSA_KV_HEADS, HEAD_DIM)
    moba_kv = moba_kv.reshape(b, t, 2, MOBA_HEADS, HEAD_DIM)
    nsa_slopes = alibi_slopes(NSA_HEADS).reshape(NSA_KV_HEADS, NSA_GROUP)
    q_pos = past + jnp.arange(t, dtype=jnp.int32)
    kc, vc, kc_end = compress_tokens(jnp.concatenate([gather_pages(cache_cmp, page_table), cmp_kv], axis=1),
                                     phi_pos, phi_w1, phi_w2)
    ks, vs = to_blocks(jnp.concatenate([gather_pages(cache_sel, page_table), sel_kv], axis=1), SEL_BLOCK)
    wb = cache_win.shape[1]
    win_all = jnp.concatenate([cache_win, win_kv], axis=1)
    kw_pos = past - wb + jnp.arange(wb + t, dtype=jnp.int32)
    o_nsa = nsa_attend(nsa_heads(q_nsa), jax.nn.sigmoid(nsa_heads(g_nsa)), q_pos, kc, vc, kc_end, ks, vs,
                       win_all[:, :, 0].transpose(0, 2, 1, 3), win_all[:, :, 1].transpose(0, 2, 1, 3),
                       kw_pos, nsa_slopes)
    kb, vb = to_blocks(jnp.concatenate([gather_pages(cache_moba, page_table), moba_kv], axis=1), MOBA_BLOCK)
    o_moba = moba_attend(split_heads(q_moba, MOBA_HEADS), q_pos, kb, vb, block_means(kb), alibi_slopes(MOBA_HEADS))
    o_mem = cross_attend(split_heads(q_mem, MEM_HEADS), cache_mem[:, :, 0].transpose(0, 2, 1, 3),
                         cache_mem[:, :, 1].transpose(0, 2, 1, 3))
    y = merge_branches(x, nsa_rows(o_nsa), z_nsa, head_rows(o_moba), z_moba, head_rows(o_mem), z_mem, g_merge,
                       w_br_nsa, w_br_moba, w_br_mem, w_out)
    keep = min(WINDOW, wb + t)
    return y, (cmp_kv, sel_kv, moba_kv, win_all[:, wb + t - keep:])

def setup_inputs(seed: int = 0) -> dict:
    key = jax.random.key(seed)
    ks = jax.random.split(key, 24)
    f32 = jnp.float32
    n_pages = PAST_LEN // PAGE_SIZE
    n_pool = (5 * DEC_BATCH * n_pages + 3) // 4
    win_rows = min(WINDOW, PAST_LEN)

    def nrm(k, shape, scale):
        return jax.random.normal(k, shape, f32) * scale

    page_table = jax.random.permutation(ks[0], n_pool)[:DEC_BATCH * n_pages].reshape(DEC_BATCH, n_pages).astype(jnp.int32)
    return {
        'x_prompt': nrm(ks[1], (BATCH, SEQ, D_MODEL), 1.0),
        'x_sample': nrm(ks[2], (DEC_BATCH, DEC_SEQ, D_MODEL), 1.0),
        'cache_cmp_kv': nrm(ks[3], (DEPTH, n_pool, PAGE_SIZE, 2, NSA_KV_HEADS, HEAD_DIM), 1.0),
        'cache_sel_kv': nrm(ks[4], (DEPTH, n_pool, PAGE_SIZE, 2, NSA_KV_HEADS, HEAD_DIM), 1.0),
        'cache_moba_kv': nrm(ks[5], (DEPTH, n_pool, PAGE_SIZE, 2, MOBA_HEADS, HEAD_DIM), 1.0),
        'cache_win_kv': nrm(ks[6], (DEPTH, DEC_BATCH, win_rows, 2, NSA_KV_HEADS, HEAD_DIM), 1.0),
        'cache_mem_kv': nrm(ks[7], (DEPTH, DEC_BATCH, N_MEM, 2, MEM_HEADS, HEAD_DIM), 1.0),
        'page_table': page_table,
        'mem_prompt': nrm(ks[8], (BATCH, N_MEM, D_MODEL), 1.0),
        'norm_g': 1.0 + nrm(ks[9], (DEPTH, D_MODEL), 0.1),
        'w_in': nrm(ks[10], (DEPTH, D_MODEL, IN_WIDTH), D_MODEL ** -0.5),
        'phi_pos': nrm(ks[11], (DEPTH, 2, CMP_LEN, HEAD_DIM), 0.1),
        'phi_w1': nrm(ks[12], (DEPTH, 2, CMP_LEN, HEAD_DIM, HEAD_DIM), (CMP_LEN * HEAD_DIM) ** -0.5),
        'phi_w2': nrm(ks[13], (DEPTH, 2, HEAD_DIM, HEAD_DIM), HEAD_DIM ** -0.5),
        'mem_norm_g': 1.0 + nrm(ks[14], (DEPTH, D_MODEL), 0.1),
        'w_mem_kv': nrm(ks[15], (DEPTH, D_MODEL, 2 * MEM_WIDTH), D_MODEL ** -0.5),
        'w_br_nsa': nrm(ks[16], (DEPTH, NSA_WIDTH, D_MODEL), NSA_WIDTH ** -0.5),
        'w_br_moba': nrm(ks[17], (DEPTH, MOBA_WIDTH, D_MODEL), MOBA_WIDTH ** -0.5),
        'w_br_mem': nrm(ks[18], (DEPTH, MEM_WIDTH, D_MODEL), MEM_WIDTH ** -0.5),
        'w_out': nrm(ks[19], (DEPTH, D_MODEL, D_MODEL), D_MODEL ** -0.5),
        'final_norm_g': 1.0 + nrm(ks[20], (D_MODEL,), 0.1),
    }

def reference(x_prompt, x_sample, cache_cmp_kv, cache_sel_kv, cache_moba_kv, cache_win_kv, cache_mem_kv,
              page_table, mem_prompt, norm_g, w_in, phi_pos, phi_w1, phi_w2, mem_norm_g, w_mem_kv,
              w_br_nsa, w_br_moba, w_br_mem, w_out, final_norm_g):
    hp = x_prompt
    hs = x_sample
    ps, ss = [], []
    for l in range(DEPTH):
        hp, st_p = prompt_layer(hp, mem_prompt, norm_g[l], w_in[l], phi_pos[l], phi_w1[l], phi_w2[l],
                                mem_norm_g[l], w_mem_kv[l], w_br_nsa[l], w_br_moba[l], w_br_mem[l], w_out[l])
        hs, st_s = sample_layer(hs, cache_cmp_kv[l], cache_sel_kv[l], cache_moba_kv[l], cache_win_kv[l],
                                cache_mem_kv[l], page_table, norm_g[l], w_in[l], phi_pos[l], phi_w1[l], phi_w2[l],
                                w_br_nsa[l], w_br_moba[l], w_br_mem[l], w_out[l])
        ps.append(st_p)
        ss.append(st_s)

    def stack(states, i):
        return jnp.stack([s[i] for s in states], axis=0)

    y_prompt = rmsnorm(hp, final_norm_g)
    y_sample = rmsnorm(hs, final_norm_g)
    return (y_prompt, y_sample, stack(ps, 0), stack(ps, 1), stack(ps, 2), stack(ps, 3), stack(ps, 4),
            stack(ss, 0), stack(ss, 1), stack(ss, 2), stack(ss, 3))


_drawn_inputs = setup_inputs


def setup_inputs(seed=0):
    import zlib

    import numpy as np

    out = dict(_drawn_inputs(seed))
    spreads = {}
    factors = {'phi_pos': 5.805}
    for name, (base, spread) in spreads.items():
        noise = np.random.default_rng([zlib.crc32(name.encode()), seed]).standard_normal(out[name].shape)
        drawn = base * np.exp(spread * noise) if base else spread * noise
        out[name] = jnp.asarray(drawn.astype(out[name].dtype))
    for name, factor in factors.items():
        out[name] = (out[name] * factor).astype(out[name].dtype)
    return out
```

```python
import numpy as np
import concourse.bass as bass
from concourse import mybir
from contextlib import ExitStack

P = 128
D_MODEL, SEQ, DEC_BATCH, DEC_SEQ, PAST, PAGE = 2048, 256, 8, 8, 256, 128
HD, NSA_H, GROUPS, MOBA_H, MEM_H, N_MEM = 128, 8, 2, 4, 4, 256
REP = NSA_H // GROUPS
CMP_LEN, CMP_STRIDE = 32, 16
N_CMP = SEQ // CMP_STRIDE - 1
EPS = 1e-6
NEG = -1e30
KB = D_MODEL // P
N_SMP = DEC_BATCH * DEC_SEQ
TOK = SEQ + N_SMP
HEADS = NSA_H + MOBA_H + MEM_H
PAGES = PAST // PAGE
KEYS_S = PAST + DEC_SEQ
SEQS = DEC_BATCH + 1
SCALE = HD ** -0.5
W_CMP, W_SEL, W_WIN, W_GN = 1024, 1536, 2048, 2560
W_ZN, W_QB, W_KB, W_ZB, W_QM, W_ZM, W_GM = 2584, 3608, 4120, 5144, 5656, 6168, 6680
NG = 3 * NSA_H

J_MEM, J_GN, J_CMP, J_Q, J_K, J_V, J_Z, J_G0, J_MRG, J_OUT, J_END = 0, 4, 5, 7, 15, 19, 23, 31, 39, 63, 71

f32 = mybir.dt.float32
f32r = mybir.dt.float32r
i32 = mybir.dt.int32
ALU = mybir.AluOpType
ACT = mybir.ActivationFunctionType
AX = mybir.AxisListType.X


class Chain:

    def __init__(self, eng, sem):
        self.eng, self.sem, self.n, self.reg, self.per, self.at = eng, sem, 0, None, 0, 0

    def loop(self, reg, per):
        self.reg, self.per, self.at = reg, per, 0

    def end(self, trips):
        assert self.at == self.per, ("chain", self.at, self.per)
        self.n += self.per * trips
        self.reg, self.at = None, 0

    def add(self, ins):
        self.at += 1
        ins.then_inc(self.sem, 1)
        return self.n + self.at if self.reg is None else self.reg * self.per + (self.n + self.at)

    def wait(self, mark):
        self.eng.wait_ge(self.sem, mark)

    def link(self, ins):
        self.wait(self.add(ins))

    def settle(self):
        self.n, self.at = self.n + self.at, 0


def build(nc, A):
    ctx = ExitStack()
    with ctx:
        def sem(name):
            return ctx.enter_context(nc.semaphore(name))

        BASE = 16512
        LIMIT = 229344
        ctx.enter_context(nc.sbuf_tensor("arena", [P, (LIMIT - BASE) // 4 - 64], f32))
        top = [BASE]

        def at(name, shape, dt, offset):
            size = 4 * int(np.prod(shape[1:]))
            assert offset % 32 == 0 and offset + size <= LIMIT - 64, (name, offset, size)
            return nc.alloc_sbuf_tensor_at(name, shape, dt, offset=offset)

        def fixed(name, shape, dt=f32):
            t = at(name, shape, dt, top[0])
            top[0] += -(-4 * int(np.prod(shape[1:])) // 32) * 32
            return t

        raw = fixed("raw", [P, 2, KB, P])
        w_hi = fixed("w_hi", [P, 2, KB, P], f32r)
        w_lo = fixed("w_lo", [P, 2, KB, P], f32r)
        h_hi = fixed("h_hi", [P, KB, TOK], f32r)
        h_lo = fixed("h_lo", [P, KB, TOK], f32r)
        ident = fixed("ident", [P, P])
        ones = fixed("ones", [P, P])
        gains = fixed("gains", [P, 3, KB])
        w_phi2 = fixed("w_phi2", [P, 2, P])
        dist = fixed("dist", [P, 2 * SEQ])
        mask_cmp = fixed("mask_cmp", [P, 2, CMP_STRIDE])
        vis_cmp = fixed("vis_cmp", [P, 2, NSA_H])
        slopes = fixed("slopes", [P, 16])
        gate_rows = fixed("gate_rows", [P, 3, NG])
        gate_smp = fixed("gate_smp", [P, DEC_BATCH])
        gate_smpc = fixed("gate_smpc", [64, DEC_BATCH])
        pages = fixed("pages", [1, DEC_BATCH * PAGES], i32)
        inv = fixed("inv", [P, TOK])
        st = fixed("st", [P, 16])
        nmx = fixed("nmx", [P, 8])
        sums = fixed("sums", [P, 8])
        rsc = fixed("rsc", [P, 8])
        used_up = top[0]
        hid = fixed("hid", [P, 2, SEQS * GROUPS * N_CMP])
        kc = fixed("kc", [P, SEQS * GROUPS, N_CMP])
        q_smp = fixed("q_smp", [P, HEADS, N_SMP])
        k_smp = fixed("k_smp", [P, 8, N_SMP])
        F = top[0]
        Z_, O_, Q_, K_, V_, G_ = F, F + 20480, F + 40960, F + 61440, F + 81920, F + 94208

        x_t = at("x_t", [P, KB, TOK], f32, Z_)
        sq_t = at("sq_t", [P, KB, TOK], f32, O_)
        m_t = at("m_t", [P, KB, N_MEM], f32, Q_)
        m_lo = at("m_lo", [P, KB, N_MEM], f32r, Q_)
        m_hi = at("m_hi", [P, KB, N_MEM], f32r, Q_ + 16384)
        cmp_t = at("cmp_t", [P, 2, 2 * SEQS + 1, SEQ], f32, Z_)
        phi = [at(f"phi{n}", [P, 8, P], f32, off) for n, off in enumerate(
            (Q_, Q_ + 4096, Q_ + 8192, Q_ + 12288, Q_ + 16384, K_ + 5120, K_ + 9216, V_))]
        q_t = at("q_t", [P, HEADS, TOK], f32, Q_)
        kv_t = at("kv_t", [P, 16, TOK], f32, K_)
        v_rows = at("v_rows", [P, 2, 12 * P], f32, V_)
        rt = at("rt", [P, 2, TOK], f32, V_)
        v_new = at("v_new", [P, 8, P], f32, G_)
        v_tmp = at("v_tmp", [P, 2, TOK], f32, G_ + 4608)
        hx = at("hx", [P, 2, 288], f32, G_)
        he = at("he", [P, 2, 288], f32, G_ + 2304)
        z_t = at("z_t", [P, HEADS, TOK], f32, Z_)
        o_t = at("o_t", [P, HEADS, TOK], f32, O_)
        g0_t = at("g0_t", [P, KB, TOK], f32, Q_)
        oz_hi = at("oz_hi", [P, HEADS, TOK], f32r, Z_)
        oz_lo = at("oz_lo", [P, HEADS, TOK], f32r, O_)
        mrg_hi = at("mrg_hi", [P, KB, TOK], f32r, K_)
        mrg_lo = at("mrg_lo", [P, KB, TOK], f32r, K_ + 20480)
        top[0] = K_
        p_sel = fixed("p_sel", [P, 384])
        p_win = fixed("p_win", [P, 384])
        p_x = fixed("p_x", [P, 2, SEQ])
        assert top[0] <= K_ + 4 * 4 * TOK
        top[0] = G_
        qn = fixed("qn", [P, SEQ])
        qx = fixed("qx", [P, SEQ])
        vn_sel = fixed("vn_sel", [P, 2, P])
        vn_win = fixed("vn_win", [P, 2, P])
        vx = fixed("vx", [P, 2, P])
        hid_g = fixed("hid_g", [P, 16])
        vc_g = fixed("vc_g", [N_CMP, P])
        p_c = fixed("p_c", [P, 2, CMP_STRIDE])
        pt_sel = fixed("pt_sel", [P, 384])
        pt_win = fixed("pt_win", [P, 384])
        pt_x = fixed("pt_x", [P, 2, SEQ])
        pt_c = fixed("pt_c", [N_CMP, 2, P])
        top[0] = K_
        kt_nsa = fixed("kt_nsa", [P, 4, KEYS_S])
        kt_moba = fixed("kt_moba", [P, 4, KEYS_S])
        kt_mem = fixed("kt_mem", [P, 4, N_MEM])
        vs_sel = fixed("vs_sel", [P, 2, 2 * P])
        vs_win = fixed("vs_win", [P, 2, 2 * P])
        vs_moba = fixed("vs_moba", [P, 2, 4 * P])
        vs_mem = fixed("vs_mem", [P, 2, 4 * P])
        vs_new = fixed("vs_new", [DEC_SEQ, 8 * P])
        qb = fixed("qb", [P, NSA_H * DEC_SEQ])
        qb_pad = fixed("qb_pad", [P, 8, 32])
        kc_b = fixed("kc_b", [P, 2, N_CMP + 1])
        hid_b = fixed("hid_b", [P, 2, N_CMP + 1])
        vc_b = fixed("vc_b", [N_CMP, 2, P])
        pb_nsa = fixed("pb_nsa", [P, KEYS_S])
        pb_moba = fixed("pb_moba", [P, KEYS_S])
        pb_mem = fixed("pb_mem", [P, N_MEM])
        pb_c = fixed("pb_c", [64, CMP_STRIDE])
        ptb = [fixed(f"ptb{n}", [P, 2, P]) for n in range(3)]
        ptb_new = [fixed(f"ptb_new{n}", [DEC_SEQ, P]) for n in range(2)]
        ptb_c = fixed("ptb_c", [N_CMP, 64])
        bias_nsa = fixed("bias_nsa", [P, KEYS_S])
        bias_moba = fixed("bias_moba", [P, KEYS_S])
        top[0] = used_up
        oz = fixed("oz", [P, 2, TOK])
        g12 = fixed("g12", [P, 2, 2, TOK])
        assert top[0] <= F
        top[0] = K_ + 40960
        bt = fixed("bt", [P, 3, TOK])
        top[0] = Z_
        y_t = fixed("y_t", [P, KB, TOK])
        y_out = fixed("y_out", [P, KB, TOK])
        y_sq = fixed("y_sq", [P, 2, TOK])
        y_ss = fixed("y_ss", [P, TOK])

        bank = [ctx.enter_context(nc.psum_tensor(f"bank{n}", [P, 512], f32)) for n in range(8)]
        W, (S0, S1, S2, P0, P1, OB) = bank[:2], bank[2:]

        gate_dram = nc.dram_tensor("gate_scratch", [N_SMP, NG], f32, kind="Internal").ap()
        vnew_dram = nc.dram_tensor("vnew_scratch", [N_SMP, 8 * P], f32, kind="Internal").ap()

        def two(name):
            return [sem(f"{name}{u}") for u in range(2)]

        raw_ready, hi_ready, lo_ready, mm_done, w_free = [two(n) for n in ("raw_ready", "hi_ready", "lo_ready", "mm_done", "w_free")]
        v_out = two("v_out")
        m_in = [sem(f"m_in{n}") for n in range(4)]
        (x_in, gains_in, ones_rdy, sq_ready, ss_done, rms_v, rms_r, norm_done, hi_x, lo_x, consts_in, g_turned, g_tanh, g_rows, pages_in, cmp_in, pos_in, phi_in, pos_zero, hid_done, hid_x, hid_e, hid_rdy, kc_done,
         kc_rdy, v_turned, v_rows_rdy, kv_out, gate_wr, gate_rd, vnew_wr, win_wr) = [sem(n) for n in (
             "x_in gains_in ones_rdy sq_ready ss_done rms_v rms_r norm_done hi_x lo_x consts_in g_turned g_tanh "
             "g_rows pages_in cmp_in pos_in phi_in pos_zero hid_done hid_x hid_e hid_rdy kc_done "
             "kc_rdy v_turned v_rows_rdy kv_out gate_wr gate_rd vnew_wr win_wr").split()]
        (staged, s_ready, vc_rdy, max_rdy, exp_done, p_ready, pt_ready, pt_copied, o_ready, o_copied, z_tanh,
         smp_saved, pt_win_copied) = [sem(n) for n in ("staged s_ready vc_rdy max_rdy exp_done p_ready pt_ready pt_copied o_ready "
                                        "o_copied z_tanh smp_saved pt_win_copied").split()]
        (b_staged, kt_in, vs_in, bs_ready, bvc_rdy, bmax_rdy, bexp_done, bp_ready, bpt_ready, bpt_copied, bo_ready,
         bo_copied, pad_zero, bias_in) = [sem(n) for n in ("b_staged kt_in vs_in bs_ready bvc_rdy bmax_rdy bexp_done bp_ready "
                                                  "bpt_ready bpt_copied bo_ready bo_copied pad_zero bias_in").split()]
        (oz_rdy, oz_hi_rdy, oz_lo_rdy, mrg_rdy, mrg_hi_rdy, mrg_lo_rdy, y_in, y_sums, y_ssd, y_v, y_r, y_rdy, y_wr) = [
            sem(n) for n in ("oz_rdy oz_hi_rdy oz_lo_rdy mrg_rdy mrg_hi_rdy mrg_lo_rdy y_in y_sums y_ssd y_v y_r "
                             "y_rdy y_wr").split()]
        dve_chain = sem("dve_chain")
        carrier = sem("carrier")

        block = ctx.enter_context(nc.Block())

        def one(t, idx, n=TOK, first=0):
            return t[:, bass.ds(idx, 1), first:first + n].rearrange("p a c -> p (a c)")

        @block.sync
        def _(sp):
            def weight_tiles(j0, j1):
                with sp.Fori(j0, j1) as j:
                    for u in range(2):
                        sp.wait_ge(lo_ready[u], j + 1)
                        sp.dma_start(raw[:, u, :, :].rearrange("p k c -> p (k c)"),
                                     A["stream"][bass.ds(j * 2 + u, 1), :, :].rearrange("a p c -> p (a c)")
                                     ).then_inc(raw_ready[u], 16)

            def compression_pages(b0, b1):
                with sp.Fori(b0, b1) as b:
                    for n in range(PAGES):
                        page = sp.value_load(pages[0:1, bass.ds(b * PAGES + n, 1)], min_val=0, max_val=A["n_pool"] - 1)
                        for c in range(2):
                            sp.dma_start(cmp_t[:, c, bass.ds(b * 2, 2), n * PAGE:(n + 1) * PAGE],
                                         A["cmp_pages"][bass.ds(page, 1), c, :, :, :].rearrange("a p g r -> p (a g) r")
                                         ).then_inc(cmp_in, 16)

            weight_tiles(J_MEM, J_GN + 1)
            sp.wait_ge(lo_x, 8)
            sp.wait_ge(pages_in, 16)
            compression_pages(0, DEC_BATCH // 2)
            weight_tiles(J_CMP, J_CMP + 1)
            compression_pages(DEC_BATCH // 2, DEC_BATCH)
            for u in range(2):
                sp.wait_ge(mm_done[u], J_GN + 1)
            for n in range(8):
                sp.dma_start(phi[n][:], A["phi_w1"][n // 4][:, 8 * (n % 4):8 * (n % 4) + 8, :]).then_inc(phi_in, 16)
            weight_tiles(J_CMP + 1, J_END)
            for n in range(4):
                sp.wait_ge(y_rdy, 4 * (n + 1))
                sp.dma_start(A["y_out"][4 * n:4 * n + 4].rearrange("t p c -> p t c"),
                             y_out[:, 4 * n:4 * n + 4, :]).then_inc(y_wr, 16)
            sp.wait_ge(y_wr, 64)

        @block.gpsimd
        def _(pool):
            for u in range(2):
                pool.sem_inc(v_out[u], 16)
            pool.dma_start(pages[:], A["page_table"]).then_inc(pages_in, 16)
            for dst, name in ((w_phi2, "phi_w2"), (dist, "dist"), (mask_cmp, "mask_cmp"),
                              (vis_cmp, "vis_cmp"), (slopes, "slopes"), (ident, "ident")):
                pool.dma_start(dst[:], A[name]).then_inc(consts_in, 16)
            pool.dma_start(A["win_old"], A["cache_win"]).then_inc(win_wr, 16)

            pool.wait_ge(lo_x, 8)
            nc.gpsimd.memset(cmp_t[:, :, 2 * SEQS, :], 0.0).then_inc(pos_zero, 1)
            pool.wait_ge(pos_zero, 1)
            pool.dma_start(cmp_t[:, :, 2 * SEQS, 0:CMP_LEN], A["phi_pos"]).then_inc(pos_in, 16)
            pool.wait_ge(g_rows, 2)
            pool.dma_start(gate_dram, gate_rows[64:P, 2, :]).then_inc(gate_wr, 16)
            pool.wait_ge(gate_wr, 16)
            src = gate_dram.rearrange("(b t) (h k) -> k h t b", t=DEC_SEQ, k=3)
            for k in range(3):
                for h in range(NSA_H):
                    if k == 0:
                        dst = gate_smpc[h * DEC_SEQ:(h + 1) * DEC_SEQ, :]
                    else:
                        r0 = (k - 1) * 64 + h * DEC_SEQ
                        dst = gate_smp[r0:r0 + DEC_SEQ, :]
                    with nc.allow_non_contiguous_dma(reason="few gates"):
                        pool.dma_start(dst, src[k, h]).then_inc(gate_rd, 16)
            for u in range(2):
                pool.wait_ge(w_free[u], J_K + 4 + 1)
            pool.dma_start(A["mem_out"][0:4].rearrange("t p c -> p t c"), kv_t[:, 12:16, 0:N_MEM]).then_inc(kv_out, 16)
            pool.dma_start(A["kv_out"][0:12].rearrange("t p c -> p t c"), kv_t[:, 0:12, :]).then_inc(kv_out, 16)
            nc.gpsimd.tensor_copy(q_smp[:], q_t[:, :, SEQ:TOK]).then_inc(smp_saved, 1)
            nc.gpsimd.tensor_copy(k_smp[:], kv_t[:, 4:12, SEQ:TOK]).then_inc(smp_saved, 1)
            pool.wait_ge(v_rows_rdy, 12 + 2)
            pool.dma_start(vnew_dram, v_new[64:P].rearrange("p t d -> p (t d)")).then_inc(vnew_wr, 16)
            pool.wait_ge(vnew_wr, 16)
            for u in range(2):
                pool.wait_ge(v_out[u], 16 * 7)
            pool.wait_ge(hid_rdy, 2)

            with pool.Fori(0, GROUPS) as g:
                with pool.Fori(0, REP) as r:
                    i = g * REP + r
                    pool.wait_ge(o_ready, i + 1)
                    for dst, src in ((qn[:], one(q_t, i, SEQ)),
                                     (qx[:], one(q_t, i + NSA_H, SEQ)),
                                     (hid_g[:, 0:N_CMP], hid[:, 1, bass.ds((g + 2 * DEC_BATCH) * N_CMP, N_CMP)]),
                                     (vn_sel[:], v_rows[:, :, bass.ds(g * P, P)]),
                                     (vn_win[:], v_rows[:, :, bass.ds(g * P + 2 * P, P)]),
                                     (vx[:], v_rows[:, :, bass.ds(i * P + 4 * P, P)])):
                        nc.gpsimd.tensor_copy(dst, src).then_inc(staged, 1)

            pool.wait_ge(kv_out, 32)
            pool.wait_ge(smp_saved, 2)
            pool.wait_ge(o_copied, NSA_H + 1)
            pool.dma_start(bias_nsa[:], A["bias_nsa"]).then_inc(bias_in, 16)
            pool.dma_start(bias_moba[:], A["bias_moba"]).then_inc(bias_in, 16)
            nc.gpsimd.memset(qb_pad[:], 0.0).then_inc(pad_zero, 1)
            pool.wait_ge(pad_zero, 1)
            with pool.Fori(0, DEC_BATCH) as b:
                pool.wait_ge(bs_ready, b * 3 + 3)
                cols = bass.ds(b * DEC_SEQ, DEC_SEQ)
                nc.gpsimd.tensor_copy(qb[:].rearrange("p (h t) -> p h t", t=DEC_SEQ), q_smp[:, 0:NSA_H, cols]).then_inc(b_staged, 1)
                nc.gpsimd.tensor_copy(kt_nsa[:, :, PAST:KEYS_S], k_smp[:, 0:4, cols]).then_inc(b_staged, 1)
                nc.gpsimd.tensor_copy(kc_b[:, :, 0:N_CMP], kc[:, bass.ds(b * 2, 2), :]).then_inc(b_staged, 1)
                nc.gpsimd.tensor_copy(kt_moba[:, :, PAST:KEYS_S], k_smp[:, 4:8, cols]).then_inc(b_staged, 1)
                nc.gpsimd.tensor_copy(qb_pad[:, :, 0:DEC_SEQ], q_smp[:, NSA_H:HEADS, cols]).then_inc(b_staged, 1)
                nc.gpsimd.tensor_copy(hid_b[:, :, 0:N_CMP],
                                      hid[:, 1, bass.ds(b * (2 * N_CMP), 2 * N_CMP)].rearrange("p (g n) -> p g n", g=2)
                                      ).then_inc(b_staged, 1)

            for u in range(2):
                pool.wait_ge(mm_done[u], J_OUT + 1)
            pool.dma_start(y_t[:], A["x_t"]).then_inc(y_in, 16)
            pool.wait_ge(mrg_rdy, KB)
            nc.gpsimd.memset(y_ss[:], 0.0).then_inc(y_sums, 1)
            with pool.Fori(0, KB // 2) as k:
                for u in range(2):
                    pool.wait_ge(w_free[u], k + (J_OUT + 2))
                    nc.gpsimd.tensor_tensor(y_sq[:, u, :], one(y_t, k * 2 + u), one(y_t, k * 2 + u), ALU.mult).then_inc(y_sums, 1)
                    pool.wait_ge(y_sums, k * 4 + (2 * u + 2))
                    nc.gpsimd.tensor_tensor(y_ss[:], y_ss[:], y_sq[:, u, :], ALU.add).then_inc(y_sums, 1)
            pool.wait_ge(win_wr, 16)
            pool.wait_ge(kv_out, 32)
            for u in range(2):
                pool.wait_ge(v_out[u], 16 * 7)

        @block.scalar
        def _(act):
            def split_hi(u, j):
                act.wait_ge(raw_ready[u], j * 16 + 16)
                act.wait_ge(mm_done[u], j + 1)
                nc.scalar.activation(w_hi[:, u], raw[:, u], ACT.Copy).then_inc(hi_ready[u], 1)

            act.sem_inc(v_rows_rdy, 2)
            for n in range(4):
                act.dma_start(m_t[:, 4 * n:4 * n + 4, :], A["m_t"][:, 4 * n:4 * n + 4, :]).then_inc(m_in[n], 16)
            act.dma_start(gains[:], A["gains"]).then_inc(gains_in, 16)
            act.dma_start(x_t[:], A["x_t"]).then_inc(x_in, 16)
            for n in range(4):
                act.wait_ge(m_in[n], 16)
                nc.scalar.activation(sq_t[:, 4 * n:4 * n + 4, 0:N_MEM], m_t[:, 4 * n:4 * n + 4, :], ACT.Square).then_inc(sq_ready, 1)
            act.wait_ge(rms_v, 1)
            nc.scalar.activation(inv[:, 0:N_MEM], rt[:, 0, 0:N_MEM], ACT.Sqrt).then_inc(rms_r, 1)
            act.wait_ge(x_in, 16)
            act.wait_ge(ss_done, 1)
            nc.scalar.activation(sq_t[:], x_t[:], ACT.Square).then_inc(sq_ready, 1)
            for n in range(4):
                act.wait_ge(norm_done, n + 1)
                nc.scalar.activation(m_hi[:, 4 * n:4 * n + 4], m_t[:, 4 * n:4 * n + 4], ACT.Copy).then_inc(hi_x, 1)
            split_hi(0, 0)
            split_hi(1, 0)
            act.wait_ge(rms_v, 2)
            nc.scalar.activation(inv[:], rt[:, 0, :], ACT.Sqrt).then_inc(rms_r, 1)

            def turned_v(u, n, idx, m, new):
                act.wait_ge(v_turned, n + 1)
                tb = (P0, P1)[u]
                if new is not None:
                    nc.scalar.activation(v_new[64:P, bass.ds(new, 1), :].rearrange("p a c -> p (a c)"),
                                         tb[64:P, 256:384], ACT.Copy)
                nc.scalar.activation(v_rows[:, :, bass.ds(idx * P, P)],
                                     tb[:, 0:256].rearrange("p (n d) -> p n d", n=2), ACT.Copy).then_inc(v_rows_rdy, 1)
                if new is None:
                    act.dma_start(A["mem_out"][bass.ds(m + 4, 1)].rearrange("a p c -> p (a c)"), v_tmp[:, u, 0:N_MEM]).then_inc(v_out[u], 16)
                else:
                    act.dma_start(A["kv_out"][bass.ds(m + 12, 1)].rearrange("a p c -> p (a c)"), v_tmp[:, u, :]).then_inc(v_out[u], 16)

            for k in range(2):
                for u in range(2):
                    split_hi(u, J_MEM + 1 + k)
                    n = 2 * k + u
                    act.wait_ge(norm_done, 5 + n)
                    nc.scalar.activation(h_hi[:, 4 * n:4 * n + 4], x_t[:, 4 * n:4 * n + 4], ACT.Copy).then_inc(hi_x, 1)
            with act.Fori(0, 2) as k:
                for u in range(2):
                    split_hi(u, k + (J_MEM + 3))
                for u in range(2):
                    turned_v(u, k * 2 + u, k * 2 + (8 + u), k * 2 + u, None)
            for u in range(2):
                split_hi(u, J_GN + 1)
            act.wait_ge(g_turned, 1)
            nc.scalar.activation(gate_rows[:], P0[:, 0:384].rearrange("p (n c) -> p n c", c=P)[:, :, 0:NG],
                                 ACT.Tanh, scale=0.5).then_inc(g_tanh, 1)
            for k in range(2):
                for u in range(2):
                    split_hi(u, J_CMP + k + 1)
            for c in range(2):
                act.wait_ge(hid_x, c + 1)
                nc.scalar.activation(he[:, c, 0:270], hx[:, c, 0:270], ACT.Tanh, scale=0.5).then_inc(hid_e, 1)
            with act.Fori(0, 12) as k:
                for u in range(2):
                    split_hi(u, k + (J_Q + 1))
            with act.Fori(0, 4) as k:
                for u in range(2):
                    split_hi(u, k + (J_V + 1))
                for u in range(2):
                    turned_v(u, k * 2 + (4 + u), k * 2 + u, k * 2 + u, k * 2 + u)

            def softmax_rows(p, n, bias):
                nc.scalar.activation(p, p, ACT.Exp, bias=bias, accum_out=sums[:, n:n + 1]).then_inc(exp_done, 1)

            with act.Fori(0, NSA_H) as i:
                act.wait_ge(max_rdy, i * 4 + 1)
                for q in range(2):
                    softmax_rows(p_c[:, q, 0:N_CMP], q, nmx[:, q:q + 1])
                act.wait_ge(max_rdy, i * 4 + 2)
                softmax_rows(p_sel[:, 0:128], 2, nmx[:, 2:3])
                softmax_rows(p_sel[:, 128:384], 3, nmx[:, 3:4])
                act.wait_ge(max_rdy, i * 4 + 3)
                softmax_rows(p_win[:, 0:128], 4, nmx[:, 4:5])
                softmax_rows(p_win[:, 128:384], 5, nmx[:, 5:6])
                act.wait_ge(max_rdy, i * 4 + 4)
                for q in range(2):
                    softmax_rows(p_x[:, q, :], 6 + q, nmx[:, 6 + q:7 + q])
                for u in range(2):
                    if u:
                        act.wait_ge(pt_ready, i * 3 + 2)
                        nc.scalar.activation(pt_c[:, 1, :], P1[0:N_CMP, 384:512], ACT.Copy)
                        nc.scalar.activation(pt_win[:], P1[:, 0:384], ACT.Copy).then_inc(pt_win_copied, 1)
                        act.wait_ge(o_ready, i + 2)
                        nc.scalar.activation(one(o_t, i, SEQ), OB[:, 0:SEQ], ACT.Copy)
                        nc.scalar.activation(one(o_t, i + NSA_H, SEQ), OB[:, SEQ:2 * SEQ], ACT.Copy).then_inc(o_copied, 1)
                    act.wait_ge(mm_done[u], i + (J_Z + 2))
                    nc.scalar.activation(one(z_t, i * 2 + u), W[u][:, 0:TOK], ACT.Tanh, scale=0.5).then_inc(z_tanh, 1)
                    split_hi(u, i + (J_Z + 1))

            def load_keys(b):
                for n in range(PAGES):
                    page = act.value_load(pages[0:1, bass.ds(b * PAGES + n, 1)], min_val=0, max_val=A["n_pool"] - 1)
                    act.dma_start(kt_nsa[:, 0:2, n * PAGE:(n + 1) * PAGE],
                                  A["sel_k"][bass.ds(page, 1)].rearrange("a p g r -> p (a g) r")).then_inc(kt_in, 16)
                    act.dma_start(kt_moba[:, :, n * PAGE:(n + 1) * PAGE],
                                  A["moba_k"][bass.ds(page, 1)].rearrange("a p g r -> p (a g) r")).then_inc(kt_in, 16)
                act.dma_start(kt_nsa[:, 2:4, 0:PAST],
                              A["win_k"][bass.ds(b, 1)].rearrange("a p g r -> p (a g) r")).then_inc(kt_in, 16)
                act.dma_start(kt_mem[:], A["mem_k"][bass.ds(b, 1)].rearrange("a p g r -> p (a g) r")).then_inc(kt_in, 16)

            def load_values(b):
                for n in range(PAGES):
                    page = act.value_load(pages[0:1, bass.ds(b * PAGES + n, 1)], min_val=0, max_val=A["n_pool"] - 1)
                    act.dma_start(vs_sel[:, n, :], A["sel_v"][bass.ds(page, 1)].rearrange("a p c -> p (a c)")).then_inc(vs_in, 16)
                    act.dma_start(vs_moba[:, n, :], A["moba_v"][bass.ds(page, 1)].rearrange("a p c -> p (a c)")).then_inc(vs_in, 16)
                act.dma_start(vs_win[:], A["win_v"][bass.ds(b, 1)].rearrange("a n p c -> p (a n) c")).then_inc(vs_in, 16)
                act.dma_start(vs_mem[:], A["mem_v"][bass.ds(b, 1)].rearrange("a n p c -> p (a n) c")).then_inc(vs_in, 16)
                act.dma_start(vs_new[:], vnew_dram[bass.ds(b * DEC_SEQ, DEC_SEQ), :]).then_inc(vs_in, 16)

            def sample_batch(b, more):
                act.wait_ge(bmax_rdy, b * 3 + 1)
                nc.scalar.activation(pb_nsa[:], pb_nsa[:], ACT.Exp, bias=nmx[:, 0:1], accum_out=sums[:, 0:1]).then_inc(bexp_done, 1)
                nc.scalar.activation(pb_c[:, 0:N_CMP], S0[0:64, 272:272 + N_CMP], ACT.Exp, bias=nmx[0:64, 1:2],
                                     accum_out=sums[0:64, 1:2]).then_inc(bexp_done, 1)
                act.wait_ge(bmax_rdy, b * 3 + 2)
                nc.scalar.activation(pb_moba[:], pb_moba[:], ACT.Exp, bias=nmx[:, 2:3], accum_out=sums[:, 2:3]).then_inc(bexp_done, 1)
                act.wait_ge(bmax_rdy, b * 3 + 3)
                nc.scalar.activation(pb_mem[:], S2[:, 0:N_MEM], ACT.Exp, bias=nmx[:, 3:4], accum_out=sums[:, 3:4]).then_inc(bexp_done, 1)
                if more:
                    load_keys(b + 1)
                for u in range(2):
                    if u:
                        act.wait_ge(bo_ready, b + 2)
                        nc.scalar.activation(o_t[:, :, bass.ds(b * DEC_SEQ + SEQ, DEC_SEQ)],
                                             OB[:, 0:P].rearrange("p (h t) -> p h t", t=DEC_SEQ), ACT.Copy).then_inc(bo_copied, 1)
                    act.wait_ge(mm_done[u], b + (J_G0 + 2))
                    nc.scalar.activation(one(g0_t, b * 2 + u), W[u][:, 0:TOK], ACT.Tanh, scale=0.5).then_inc(w_free[u], 1)
                    split_hi(u, b + (J_G0 + 1))
                if more:
                    load_values(b + 1)

            act.wait_ge(kv_out, 32)
            act.wait_ge(smp_saved, 2)
            act.wait_ge(o_copied, NSA_H + 1)
            load_keys(0)
            load_values(0)
            with act.Fori(0, DEC_BATCH - 1) as b:
                sample_batch(b, True)
            sample_batch(DEC_BATCH - 1, False)

            with act.Fori(0, HEADS // 2) as k:
                for u in range(2):
                    act.wait_ge(oz_rdy, k * 2 + u + 1)
                    nc.scalar.activation(one(oz_hi, k * 2 + u), oz[:, u, :], ACT.Copy).then_inc(oz_hi_rdy, 1)

            with act.Fori(0, KB // 2) as k:
                for br in range(2):
                    for u in range(2):
                        act.wait_ge(mm_done[u], k * 3 + (J_MRG + br + 2))
                        if br == 0:
                            act.wait_ge(w_free[u], k * 3 + (J_MRG + 1))
                        nc.scalar.activation(g12[:, u, br, :], W[u][:, 0:TOK], ACT.Tanh, scale=0.5).then_inc(w_free[u], 1)
                        split_hi(u, k * 3 + (J_MRG + br + 1))
                for u in range(2):
                    split_hi(u, k * 3 + (J_MRG + 3))
                    act.wait_ge(mrg_rdy, k * 2 + u + 1)
                    nc.scalar.activation(one(mrg_hi, k * 2 + u), bt[:, 0, :], ACT.Copy).then_inc(mrg_hi_rdy, 1)
            with act.Fori(0, KB // 2 - 1) as k:
                for u in range(2):
                    split_hi(u, k + (J_OUT + 1))
            act.wait_ge(y_v, 1)
            nc.scalar.activation(inv[:], rt[:, 0, :], ACT.Sqrt).then_inc(y_r, 1)

        @block.vector
        def _(dve):
            ch = Chain(dve, dve_chain)

            def split_lo(u, j):
                dve.wait_ge(hi_ready[u], j + 1)
                nc.vector.tensor_tensor(w_lo[:, u], raw[:, u], w_hi[:, u].bitcast(f32), ALU.subtract).then_inc(lo_ready[u], 1)

            for u in range(2):
                dve.sem_inc(lo_ready[u], 1)
                dve.sem_inc(w_free[u], 1)
            dve.sem_inc(oz_lo_rdy, 2)
            dve.sem_inc(mrg_lo_rdy, 1)
            nc.vector.memset(ones[:], 1.0).then_inc(ones_rdy, 1)

            def inverse_root(n, total, v_sem, r_sem, count):
                v, t, y = rt[:, 0, 0:n], rt[:, 1, 0:n], inv[:, 0:n]
                nc.vector.tensor_scalar(v, total, 1.0 / D_MODEL, EPS, ALU.mult, ALU.add).then_inc(v_sem, 1)
                dve.wait_ge(r_sem, count)
                ch.link(nc.vector.reciprocal(y, y))
                ch.link(nc.vector.tensor_tensor(t, y, y, ALU.mult))
                ch.link(nc.vector.tensor_tensor(t, t, v, ALU.mult))
                ch.link(nc.vector.tensor_scalar(t, t, -0.5, 1.5, ALU.mult, ALU.add))
                ch.link(nc.vector.tensor_tensor(y, y, t, ALU.mult))

            dve.wait_ge(gains_in, 16)
            dve.wait_ge(ss_done, 1)
            inverse_root(N_MEM, S0[:, 0:N_MEM], rms_v, rms_r, 1)

            def norm_part(x, n, gain, cols):
                for kb in range(4 * n, 4 * n + 4):
                    last = nc.vector.scalar_tensor_tensor(x[:, kb, :], x[:, kb, :], gains[:, gain, kb:kb + 1], inv[:, 0:cols],
                                                          ALU.mult, ALU.mult)
                last.then_inc(norm_done, 1)

            def low_part(lo, x, hi, n, count):
                dve.wait_ge(hi_x, count)
                nc.vector.tensor_tensor(lo[:, 4 * n:4 * n + 4], x[:, 4 * n:4 * n + 4], hi[:, 4 * n:4 * n + 4].bitcast(f32),
                                        ALU.subtract).then_inc(lo_x, 1)

            for n in range(5):
                if n < 4:
                    norm_part(m_t, n, 1, N_MEM)
                if n:
                    dve.wait_ge(norm_done, n)
                    low_part(m_lo, m_t, m_hi, n - 1, n)
            split_lo(0, 0)
            split_lo(1, 0)
            dve.wait_ge(ss_done, 2)
            inverse_root(TOK, S1[:, 0:TOK], rms_v, rms_r, 2)
            norm_part(x_t, 0, 0, TOK)
            ch.settle()

            for k in range(2):
                for u in range(2):
                    n = 2 * k + u
                    dve.wait_ge(mm_done[u], J_MEM + 2 + k)
                    nc.vector.tensor_copy(kv_t[:, 12 + n, 0:N_MEM], W[u][:, 0:N_MEM]).then_inc(w_free[u], 1)
                    split_lo(u, J_MEM + 1 + k)
                    if n < 3:
                        norm_part(x_t, n + 1, 0, TOK)
                    low_part(h_lo, x_t, h_hi, n, 5 + n)

            def value_tile(u, j, m, n):
                dve.wait_ge(mm_done[u], j + 2)
                dve.wait_ge(v_out[u], m * 16 + 16)
                nc.vector.tensor_copy(v_tmp[:, u, 0:n], W[u][:, 0:n]).then_inc(w_free[u], 1)
                split_lo(u, j + 1)

            with dve.Fori(0, 2) as k:
                for u in range(2):
                    value_tile(u, k + (J_MEM + 2), k, N_MEM)
            value_tile(0, J_GN, 2, TOK)
            dve.wait_ge(mm_done[1], J_GN + 2)
            dve.sem_inc(w_free[1], 1)
            split_lo(1, J_GN + 1)
            dve.wait_ge(g_tanh, 1)
            nc.vector.tensor_scalar(gate_rows[:], gate_rows[:], 0.5, 0.5, ALU.mult, ALU.add).then_inc(g_rows, 1)
            dve.wait_ge(g_rows, 1)
            dve.wait_ge(consts_in, 6 * 16)
            gc = gate_rows[:, 0:2, :].rearrange("p q (h k) -> p q h k", k=3)[:, :, :, 0]
            nc.vector.tensor_tensor(gc, gc, vis_cmp[:], ALU.mult).then_inc(g_rows, 1)
            dve.wait_ge(lo_x, 8)
            for k in range(2):
                for u in range(2):
                    dve.wait_ge(mm_done[u], J_CMP + k + 2)
                    nc.vector.tensor_copy(kv_t[:, 2 * k + u, :], W[u][:, 0:TOK])
                    nc.vector.tensor_copy(cmp_t[:, k, 2 * DEC_BATCH + u, :], W[u][:, 0:SEQ]).then_inc(w_free[u], 1)
                    split_lo(u, J_CMP + k + 1)
            for c in range(2):
                dve.wait_ge(hid_done, c + 1)
                ch.link(nc.vector.tensor_copy(st[:, c:c + 1], (S0, S1)[c][:, 270:271]))
                nc.vector.tensor_scalar_add(hx[:, c, 0:270], (S0, S1)[c][:, 0:270], st[:, c:c + 1]).then_inc(hid_x, 1)
            for c in range(2):
                dve.wait_ge(hid_e, c + 1)
                ch.link(nc.vector.tensor_scalar(he[:, c, 0:270], he[:, c, 0:270], 0.5, 0.5, ALU.mult, ALU.add))
                nc.vector.tensor_tensor(hid[:, c, :], hx[:, c, 0:270], he[:, c, 0:270], ALU.mult).then_inc(hid_rdy, 1)
            with dve.Fori(0, 8) as k:
                for u in range(2):
                    dve.wait_ge(mm_done[u], k + (J_Q + 2))
                    nc.vector.tensor_scalar_mul(one(q_t, k * 2 + u), W[u][:, 0:TOK], SCALE).then_inc(w_free[u], 1)
                    split_lo(u, k + (J_Q + 1))
            dve.wait_ge(kc_done, 1)
            nc.vector.tensor_copy(kc[:].rearrange("p s n -> p (s n)"), S2[:, 0:270]).then_inc(kc_rdy, 1)
            with dve.Fori(0, 4) as k:
                for u in range(2):
                    dve.wait_ge(mm_done[u], k + (J_K + 2))
                    nc.vector.tensor_copy(one(kv_t, k * 2 + (4 + u)), W[u][:, 0:TOK]).then_inc(w_free[u], 1)
                    split_lo(u, k + (J_K + 1))
            with dve.Fori(0, 4) as k:
                for u in range(2):
                    value_tile(u, k + J_V, k + 2, TOK)

            ch.settle()
            with dve.Fori(0, NSA_H) as i:
                ch.loop(i, 6)
                slope = slopes[:, bass.ds(i, 1)]
                slope_x = slopes[:, bass.ds(i + NSA_H, 1)]
                dve.wait_ge(s_ready, i * 3 + 1)
                ch.link(nc.vector.tensor_tensor(p_c[:, :, 0:N_CMP],
                                                S0[:, 384:416].rearrange("p (q n) -> p q n", q=2)[:, :, 0:N_CMP],
                                                mask_cmp[:, :, 0:N_CMP], ALU.add))
                nc.vector.reduce_max(nmx[:, 0:2], p_c[:, :, 0:N_CMP], AX, negate=True).then_inc(max_rdy, 1)
                ch.link(nc.vector.scalar_tensor_tensor(p_sel[:], dist[:, 128:512], slope, S0[:, 0:384], ALU.mult, ALU.add))
                nc.vector.reduce_max(nmx[:, 2:3], p_sel[:, 0:128], AX, negate=True)
                nc.vector.reduce_max(nmx[:, 3:4], p_sel[:, 128:384], AX, negate=True).then_inc(max_rdy, 1)
                dve.wait_ge(s_ready, i * 3 + 2)
                ch.link(nc.vector.scalar_tensor_tensor(p_win[:], dist[:, 128:512], slope, S1[:, 0:384], ALU.mult, ALU.add))
                nc.vector.reduce_max(nmx[:, 4:5], p_win[:, 0:128], AX, negate=True)
                nc.vector.reduce_max(nmx[:, 5:6], p_win[:, 128:384], AX, negate=True).then_inc(max_rdy, 1)
                nc.vector.tensor_copy(vc_g[:], S1[0:N_CMP, 384:512]).then_inc(vc_rdy, 1)
                dve.wait_ge(s_ready, i * 3 + 3)
                ch.link(nc.vector.scalar_tensor_tensor(p_x[:].rearrange("p q n -> p (q n)"),
                                                       dist[:], slope_x, S2[:],
                                                       ALU.mult, ALU.add))
                nc.vector.reduce_max(nmx[:, 6:8], p_x[:], AX, negate=True).then_inc(max_rdy, 1)
                dve.wait_ge(exp_done, i * 8 + 6)
                ch.link(nc.vector.reciprocal(rsc[:, 0:6], sums[:, 0:6]))

                def scale_p(p, n, q, br):
                    return nc.vector.tensor_scalar(p, p, rsc[:, n:n + 1], gate_rows[:, q, bass.ds(i * 3 + br, 1)],
                                                   ALU.mult, ALU.mult)

                scale_p(p_c[:, 0, 0:N_CMP], 0, 0, 0)
                scale_p(p_c[:, 1, 0:N_CMP], 1, 1, 0)
                scale_p(p_sel[:, 0:128], 2, 0, 1)
                scale_p(p_sel[:, 128:384], 3, 1, 1).then_inc(p_ready, 1)
                scale_p(p_win[:, 0:128], 4, 0, 2)
                scale_p(p_win[:, 128:384], 5, 1, 2).then_inc(p_ready, 1)
                dve.wait_ge(exp_done, i * 8 + 8)
                ch.link(nc.vector.reciprocal(rsc[:, 6:8], sums[:, 6:8]))
                nc.vector.tensor_scalar_mul(p_x[:, 0, :], p_x[:, 0, :], rsc[:, 6:7])
                nc.vector.tensor_scalar_mul(p_x[:, 1, :], p_x[:, 1, :], rsc[:, 7:8]).then_inc(p_ready, 1)

                def z_tile(u):
                    dve.wait_ge(z_tanh, i * 2 + (u + 1))
                    nc.vector.scalar_tensor_tensor(one(z_t, i * 2 + u), one(z_t, i * 2 + u), 1.0, W[u][:, 0:TOK],
                                                   ALU.add, ALU.mult).then_inc(w_free[u], 1)
                    split_lo(u, i + (J_Z + 1))

                z_tile(0)
                dve.wait_ge(pt_ready, i * 3 + 1)
                nc.vector.tensor_copy(pt_c[:, 0, :], P0[0:N_CMP, 384:512])
                nc.vector.tensor_copy(pt_sel[:], P0[:, 0:384]).then_inc(pt_copied, 1)
                dve.wait_ge(pt_ready, i * 3 + 3)
                nc.vector.tensor_copy(pt_x[:].rearrange("p n q -> p (n q)"), P0[:]).then_inc(pt_copied, 1)
                z_tile(1)
                ch.end(NSA_H)

            dve.wait_ge(bias_in, 32)
            with dve.Fori(0, DEC_BATCH) as b:
                ch.loop(b, 4)
                dve.wait_ge(bs_ready, b * 3 + 4)
                nc.vector.reduce_max(nmx[0:64, 1:2], S0[0:64, 272:272 + N_CMP], AX, negate=True)
                ch.link(nc.vector.tensor_tensor_reduce(out=pb_nsa[:], in0=S0[:, 0:KEYS_S], in1=bias_nsa[:], scale=1.0,
                                                       scalar=NEG, op0=ALU.add, op1=ALU.max, accum_out=st[:, 2:3]))
                dve.wait_ge(bs_ready, b * 3 + 5)
                nc.vector.tensor_scalar_mul(nmx[:, 0:1], st[:, 2:3], -1.0).then_inc(bmax_rdy, 1)
                ch.link(nc.vector.tensor_tensor_reduce(out=pb_moba[:], in0=S1[:, 0:KEYS_S], in1=bias_moba[:], scale=1.0,
                                                       scalar=NEG, op0=ALU.add, op1=ALU.max, accum_out=st[:, 3:4]))
                nc.vector.tensor_scalar_mul(nmx[:, 2:3], st[:, 3:4], -1.0).then_inc(bmax_rdy, 1)
                dve.wait_ge(bs_ready, b * 3 + 6)
                nc.vector.tensor_copy(vc_b[:].rearrange("p g d -> p (g d)"), S2[0:N_CMP, 256:512]).then_inc(bvc_rdy, 1)
                nc.vector.reduce_max(nmx[:, 3:4], S2[:, 0:N_MEM], AX, negate=True).then_inc(bmax_rdy, 1)
                dve.wait_ge(bexp_done, b * 4 + 2)
                nc.vector.reciprocal(rsc[:, 0:1], sums[:, 0:1])
                ch.link(nc.vector.reciprocal(rsc[0:64, 1:2], sums[0:64, 1:2]))
                nc.vector.tensor_scalar(pb_nsa[:], pb_nsa[:], rsc[:, 0:1], gate_smp[:, bass.ds(b, 1)], ALU.mult, ALU.mult)
                nc.vector.tensor_scalar(pb_c[:, 0:N_CMP], pb_c[:, 0:N_CMP], rsc[0:64, 1:2], gate_smpc[:, bass.ds(b, 1)],
                                        ALU.mult, ALU.mult).then_inc(bp_ready, 1)
                dve.wait_ge(bexp_done, b * 4 + 4)
                nc.vector.reciprocal(rsc[:, 2:3], sums[:, 2:3])
                ch.link(nc.vector.reciprocal(rsc[:, 3:4], sums[:, 3:4]))
                nc.vector.tensor_scalar_mul(pb_moba[:], pb_moba[:], rsc[:, 2:3]).then_inc(bp_ready, 1)
                nc.vector.tensor_scalar_mul(pb_mem[:], pb_mem[:], rsc[:, 3:4]).then_inc(bp_ready, 1)

                split_lo(0, b + (J_G0 + 1))
                for n in range(3):
                    dve.wait_ge(bpt_ready, b * 3 + (n + 1))
                    pt = (P0, P1, P0)[n]
                    if n < 2:
                        nc.vector.tensor_copy(ptb_new[n][:], pt[0:DEC_SEQ, 256:384])
                    if n == 0:
                        nc.vector.tensor_copy(ptb_c[:], pt[0:N_CMP, 384:448])
                    nc.vector.tensor_copy(ptb[n][:].rearrange("p n c -> p (n c)"), pt[:, 0:256]).then_inc(bpt_copied, 1)
                split_lo(1, b + (J_G0 + 1))
                ch.end(DEC_BATCH)

            dve.wait_ge(o_copied, NSA_H + 1)
            dve.wait_ge(bo_copied, DEC_BATCH + 1)
            with dve.Fori(0, HEADS // 2) as k:
                for u in range(2):
                    dve.wait_ge(oz_lo_rdy, k * 2 + (u + 1))
                    nc.vector.scalar_tensor_tensor(oz[:, u, :], one(o_t, k * 2 + u), 0.5, one(z_t, k * 2 + u), ALU.mult,
                                                   ALU.mult).then_inc(oz_rdy, 1)
                for u in range(2):
                    dve.wait_ge(oz_hi_rdy, k * 2 + (u + 1))
                    nc.vector.tensor_tensor(one(oz_lo, k * 2 + u), oz[:, u, :], one(oz_hi, k * 2 + u).bitcast(f32),
                                            ALU.subtract).then_inc(oz_lo_rdy, 1)

            with dve.Fori(0, KB // 2) as k:
                ch.loop(k, 4)
                for br in range(2):
                    for u in range(2):
                        split_lo(u, k * 3 + (J_MRG + br + 1))
                for u in range(2):
                    banks = ((S0, S1, S2), (P0, P1, OB))[u]
                    dve.wait_ge(mm_done[u], k * 3 + (J_MRG + 4))
                    dve.wait_ge(w_free[u], k * 3 + (J_MRG + 3))
                    dve.wait_ge(mrg_lo_rdy, k * 2 + (u + 1))
                    nc.vector.scalar_tensor_tensor(bt[:, 0, :], one(g0_t, k * 2 + u), 1.0, banks[0][:, 0:TOK], ALU.add, ALU.mult)
                    ch.link(nc.vector.scalar_tensor_tensor(bt[:, 1, :], g12[:, u, 0, :], 1.0, banks[1][:, 0:TOK], ALU.add, ALU.mult))
                    nc.vector.scalar_tensor_tensor(bt[:, 2, :], g12[:, u, 1, :], 1.0, banks[2][:, 0:TOK], ALU.add,
                                                   ALU.mult).then_inc(w_free[u], 1)
                    ch.link(nc.vector.tensor_tensor(bt[:, 0, :], bt[:, 0, :], bt[:, 1, :], ALU.add))
                    dve.wait_ge(w_free[u], k * 3 + (J_MRG + 4))
                    nc.vector.tensor_tensor(bt[:, 0, :], bt[:, 0, :], bt[:, 2, :], ALU.add).then_inc(mrg_rdy, 1)
                    split_lo(u, k * 3 + (J_MRG + 3))
                    dve.wait_ge(mrg_hi_rdy, k * 2 + (u + 1))
                    nc.vector.tensor_tensor(one(mrg_lo, k * 2 + u), bt[:, 0, :], one(mrg_hi, k * 2 + u).bitcast(f32),
                                            ALU.subtract).then_inc(mrg_lo_rdy, 1)
                ch.end(KB // 2)

            dve.wait_ge(y_in, 16)
            with dve.Fori(0, KB // 2 - 1) as k:
                for u in range(2):
                    dve.wait_ge(mm_done[u], k + (J_OUT + 2))
                    nc.vector.scalar_tensor_tensor(one(y_t, k * 2 + u), W[u][:, 0:TOK], 0.5, one(y_t, k * 2 + u), ALU.mult,
                                                   ALU.add).then_inc(w_free[u], 1)
                    split_lo(u, k + (J_OUT + 1))
            for u in range(2):
                dve.wait_ge(mm_done[u], J_END + 1)
                nc.vector.scalar_tensor_tensor(y_t[:, KB - 2 + u, :], W[u][:, 0:TOK], 0.5, y_t[:, KB - 2 + u, :], ALU.mult,
                                               ALU.add).then_inc(w_free[u], 1)
            dve.wait_ge(y_ssd, 1)
            inverse_root(TOK, S0[:, 0:TOK], y_v, y_r, 1)
            for kb in range(KB):
                nc.vector.scalar_tensor_tensor(y_out[:, kb, :], y_t[:, kb, :], gains[:, 2, kb:kb + 1], inv[:],
                                               ALU.mult, ALU.mult).then_inc(y_rdy, 1)

        @block.tensor
        def _(pe):
            for u in range(2):
                pe.sem_inc(mm_done[u], 1)
            pe.sem_inc(o_ready, 1)
            pe.sem_inc(bs_ready, 3)
            pe.sem_inc(bo_ready, 1)
            pe.sem_inc(o_copied, 1)
            pe.sem_inc(bo_copied, 1)

            def part(u, j, hi, lo, n, kbs, out=None, first=0, last=KB - 1):
                out = W[u] if out is None else out
                if kbs[0] == 0:
                    pe.wait_ge(lo_ready[u], j + 2)
                    pe.wait_ge(w_free[u], j + 1)
                for kb in kbs:
                    nc.tensor.matmul(out[:, 0:n], w_hi[:, u, kb, :], hi[:, kb, :], start=(kb == first), stop=False)
                    nc.tensor.matmul(out[:, 0:n], w_hi[:, u, kb, :], lo[:, kb, :], start=False, stop=False)
                    mm = nc.tensor.matmul(out[:, 0:n], w_lo[:, u, kb, :], hi[:, kb, :], start=False, stop=(kb == last))
                if kbs[-1] == KB - 1:
                    mm.then_inc(mm_done[u], 1)

            ALL, PART_A, PART_B, PART_C = range(KB), range(0, 5), range(5, 10), range(10, KB)

            pe.wait_ge(ones_rdy, 1)
            for n, (out, cols) in enumerate(((S0, N_MEM), (S1, TOK))):
                for kb in range(KB):
                    if n == 0 and kb % 4 == 0:
                        pe.wait_ge(sq_ready, kb // 4 + 1)
                    elif kb == 0:
                        pe.wait_ge(sq_ready, 5)
                    mm = nc.tensor.matmul(out[:, 0:cols], ones[:], sq_t[:, kb, 0:cols], start=(kb == 0), stop=(kb == KB - 1))
                mm.then_inc(ss_done, 1)

            def turn_value(u, n, blocks):
                pe.wait_ge(v_rows_rdy, n + 1)
                for m, first in enumerate((0, P, TOK - P)[:blocks]):
                    mm = nc.tensor.transpose((P0, P1)[u][:, m * P:(m + 1) * P], v_tmp[:, u, first:first + P], ident[:])
                mm.then_inc(v_turned, 1)

            pe.wait_ge(lo_x, 4)
            with pe.Fori(0, 2) as k:
                for u in range(2):
                    part(u, k + J_MEM, m_hi, m_lo, N_MEM, ALL)
            pe.wait_ge(consts_in, 6 * 16)
            with pe.Fori(0, 2) as k:
                for u in range(2):
                    part(u, k + (J_MEM + 2), m_hi, m_lo, N_MEM, ALL)
                for u in range(2):
                    pe.wait_ge(w_free[u], k + (J_MEM + 4))
                    turn_value(u, k * 2 + u, 2)
            pe.wait_ge(lo_x, 8)
            part(0, J_GN, h_hi, h_lo, TOK, ALL)
            pe.wait_ge(lo_ready[1], J_GN + 2)
            pe.wait_ge(mm_done[0], J_GN + 2)
            pe.sem_inc(mm_done[1], 1)
            part(0, J_CMP, h_hi, h_lo, TOK, ALL)
            pe.wait_ge(v_rows_rdy, 5)
            for m, first in enumerate((0, P, TOK - P)):
                mm = nc.tensor.transpose(P0[:, m * P:(m + 1) * P], v_tmp[:, 0, first:first + P], ident[:])
            mm.then_inc(g_turned, 1)
            part(1, J_CMP, h_hi, h_lo, TOK, ALL)
            for u in range(2):
                part(u, J_CMP + 1, h_hi, h_lo, TOK, ALL)
            for u in range(2):
                pe.wait_ge(w_free[u], J_Q + 1)
            pe.wait_ge(cmp_in, 16 * PAGES * 2 * DEC_BATCH)
            pe.wait_ge(pos_in, 16)
            pe.wait_ge(phi_in, 8 * 16)
            blocks = cmp_t[:].rearrange("p c q (n s) -> p c q n s", s=CMP_STRIDE)
            for c in range(2):
                out = (S0, S1)[c][:, 0:(2 * SEQS + 1) * N_CMP].rearrange("p (q n) -> p q n", n=N_CMP)
                for m in range(2):
                    for s in range(CMP_STRIDE):
                        mm = nc.tensor.matmul(out, phi[4 * c + 2 * m + s // 8][:, s % 8, :], blocks[:, c, :, m:m + N_CMP, s],
                                              start=(m + s == 0), stop=(m == 1 and s == CMP_STRIDE - 1))
                mm.then_inc(hid_done, 1)
            with pe.Fori(0, 8) as k:
                for u in range(2):
                    part(u, k + J_Q, h_hi, h_lo, TOK, ALL)
            pe.wait_ge(hid_rdy, 1)
            nc.tensor.matmul(S2[:, 0:270], w_phi2[:, 0, :], hid[:, 0, :], start=True, stop=True).then_inc(kc_done, 1)
            with pe.Fori(0, 4) as k:
                for u in range(2):
                    part(u, k + J_K, h_hi, h_lo, TOK, ALL)
            pe.wait_ge(g_tanh, 1)
            with pe.Fori(0, 4) as k:
                for u in range(2):
                    part(u, k + J_V, h_hi, h_lo, TOK, ALL)
                for u in range(2):
                    pe.wait_ge(w_free[u], k + (J_V + 2))
                    turn_value(u, k * 2 + (u + 4), 3)

            pe.wait_ge(kc_rdy, 1)
            with pe.Fori(0, GROUPS) as g:
                with pe.Fori(0, REP) as r:
                    i = g * REP + r
                    part(0, i + J_Z, h_hi, h_lo, TOK, PART_A)
                    pe.wait_ge(staged, i * 6 + 6)
                    kcg = kc[:, bass.ds(g + 2 * DEC_BATCH, 1), :].rearrange("p a n -> p (a n)")
                    for q in range(2):
                        nc.tensor.matmul(S0[:, 384 + 16 * q:384 + 16 * q + N_CMP], qn[:, q * P:(q + 1) * P], kcg, start=True, stop=True)
                    for bk, tile_k in ((S0, g + 4), (S1, g + 6)):
                        nc.tensor.matmul(bk[:, 0:128], qn[:, 0:P], one(kv_t, tile_k, P), start=True, stop=True)
                        mm = nc.tensor.matmul(bk[:, 128:384], qn[:, P:SEQ], one(kv_t, tile_k, SEQ), start=True, stop=True)
                        if bk is S0:
                            mm.then_inc(s_ready, 1)
                    nc.tensor.matmul(S1[0:N_CMP, 384:512], hid_g[:, 0:N_CMP], w_phi2[:, 1, :], start=True, stop=True).then_inc(s_ready, 1)
                    nc.tensor.matmul(S2[:, 0:P], qx[:, 0:P], one(kv_t, i + 8, P, P), start=True, stop=True)
                    nc.tensor.matmul(S2[:, P:SEQ], qx[:, 0:P], one(kv_t, i + 8, P), start=True, stop=True)
                    mm = nc.tensor.matmul(S2[:, SEQ:2 * SEQ], qx[:, P:SEQ], one(kv_t, i + 8, SEQ), start=True, stop=True)
                    mm.then_inc(s_ready, 1)
                    part(0, i + J_Z, h_hi, h_lo, TOK, PART_B)
                    part(0, i + J_Z, h_hi, h_lo, TOK, PART_C)
                    for n, (bk, p) in enumerate(((P0, p_sel), (P1, p_win))):
                        pe.wait_ge(p_ready, i * 3 + (n + 1))
                        nc.tensor.matmul(bk[0:N_CMP, 384:512], p_c[:, n, 0:N_CMP], ident[:], start=True, stop=True)
                        for m in range(3):
                            mm = nc.tensor.transpose(bk[:, m * P:(m + 1) * P], p[:, m * P:(m + 1) * P], ident[:])
                        mm.then_inc(pt_ready, 1)
                    part(1, i + J_Z, h_hi, h_lo, TOK, PART_A)
                    pe.wait_ge(pt_copied, i * 2 + 1)
                    pe.wait_ge(o_copied, i + 1)
                    nc.tensor.matmul(OB[:, 0:SEQ], vn_sel[:, 0, :], pt_sel[:, 0:SEQ], start=True, stop=False)
                    nc.tensor.matmul(OB[:, P:SEQ], vn_sel[:, 1, :], pt_sel[:, SEQ:384], start=False, stop=False)
                    pe.wait_ge(p_ready, i * 3 + 3)
                    for kb in range(2):
                        for q in range(2):
                            mm = nc.tensor.transpose(P0[:, kb * SEQ + q * P:kb * SEQ + (q + 1) * P], p_x[:, q, P * (kb ^ (1 - q)):P * (kb ^ (1 - q)) + P], ident[:])
                    mm.then_inc(pt_ready, 1)
                    pe.wait_ge(pt_win_copied, i + 1)
                    nc.tensor.matmul(OB[:, 0:SEQ], vn_win[:, 0, :], pt_win[:, 0:SEQ], start=False, stop=False)
                    nc.tensor.matmul(OB[:, P:SEQ], vn_win[:, 1, :], pt_win[:, SEQ:384], start=False, stop=False)
                    pe.wait_ge(vc_rdy, i + 1)
                    nc.tensor.matmul(OB[:, 0:SEQ], vc_g[:], pt_c[:].rearrange("p q c -> p (q c)"), start=False, stop=True)
                    part(1, i + J_Z, h_hi, h_lo, TOK, PART_B)
                    pe.wait_ge(pt_copied, i * 2 + 2)
                    for kb in range(2):
                        mm = nc.tensor.matmul(OB[:, SEQ:2 * SEQ], vx[:, kb, :], pt_x[:, kb, :], start=(kb == 0), stop=(kb == 1))
                    mm.then_inc(o_ready, 1)
                    part(1, i + J_Z, h_hi, h_lo, TOK, PART_C)

            pe.wait_ge(gate_rd, 16)
            with pe.Fori(0, DEC_BATCH) as b:
                part(0, b + J_G0, h_hi, h_lo, TOK, PART_A)
                pe.wait_ge(b_staged, b * 6 + 6)
                pe.wait_ge(kt_in, b * 96 + 96)
                for g in range(GROUPS):
                    nc.tensor.matmul(S0[32 * g:32 * g + 32, 272:272 + N_CMP], qb[:, 32 * g:32 * g + 32], kc_b[:, g, 0:N_CMP], start=True, stop=True)
                for n in range(4):
                    g = n % 2
                    mm = nc.tensor.matmul(S0[32 * n:32 * n + 32, 0:KEYS_S], qb[:, 32 * g:32 * g + 32], kt_nsa[:, n, :], start=True, stop=True)
                mm.then_inc(bs_ready, 1)
                for h in range(MOBA_H):
                    mm = nc.tensor.matmul(S1[32 * h:32 * h + 32, 0:KEYS_S], qb_pad[:, h, :], kt_moba[:, h, :], start=True, stop=True)
                mm.then_inc(bs_ready, 1)
                for g in range(GROUPS):
                    nc.tensor.matmul(S2[0:N_CMP, 256 + g * P:256 + (g + 1) * P], hid_b[:, g, 0:N_CMP], w_phi2[:, 1, :], start=True, stop=True)
                for h in range(MEM_H):
                    mm = nc.tensor.matmul(S2[32 * h:32 * h + 32, 0:N_MEM], qb_pad[:, MOBA_H + h, :], kt_mem[:, h, :], start=True, stop=True)
                mm.then_inc(bs_ready, 1)
                part(0, b + J_G0, h_hi, h_lo, TOK, PART_B)
                part(0, b + J_G0, h_hi, h_lo, TOK, PART_C)

                def turn(n, bk, p, new):
                    pe.wait_ge(bp_ready, b * 3 + (n + 1))
                    if new:
                        nc.tensor.matmul(bk[0:DEC_SEQ, 256:384], p[:, PAST:KEYS_S], ident[:], start=True, stop=True)
                    if n == 0:
                        nc.tensor.matmul(bk[0:N_CMP, 384:448], pb_c[:, 0:N_CMP], ident[0:64, 0:64], start=True, stop=True)
                    for m in range(2):
                        mm = nc.tensor.transpose(bk[:, m * P:(m + 1) * P], p[:, m * P:(m + 1) * P], ident[:])
                    mm.then_inc(bpt_ready, 1)

                turn(0, P0, pb_nsa, True)
                turn(1, P1, pb_moba, True)
                part(1, b + J_G0, h_hi, h_lo, TOK, PART_A)
                pe.wait_ge(bpt_copied, b * 3 + 1)
                pe.wait_ge(vs_in, b * 112 + 112)
                pe.wait_ge(bvc_rdy, b + 1)
                pe.wait_ge(bo_copied, b + 1)
                for g in range(GROUPS):
                    out = OB[:, 32 * g:32 * g + 32]
                    for s, vs in enumerate((vs_sel, vs_win)):
                        c0 = 32 * (2 * s + g)
                        for m in range(2):
                            nc.tensor.matmul(out, vs[:, m, g * P:(g + 1) * P], ptb[0][:, m, c0:c0 + 32], start=(s + m == 0), stop=False)
                        nc.tensor.matmul(out, vs_new[:, (2 * s + g) * P:(2 * s + g + 1) * P], ptb_new[0][:, c0:c0 + 32], start=False, stop=False)
                    nc.tensor.matmul(out, vc_b[:, g, :], ptb_c[:, 32 * g:32 * g + 32], start=False, stop=True)
                turn(2, P0, pb_mem, False)
                part(1, b + J_G0, h_hi, h_lo, TOK, PART_B)
                pe.wait_ge(bpt_copied, b * 3 + 3)
                for h in range(MOBA_H):
                    out = OB[:, 64 + 8 * h:72 + 8 * h]
                    for m in range(2):
                        nc.tensor.matmul(out, vs_moba[:, m, h * P:(h + 1) * P], ptb[1][:, m, 32 * h:32 * h + 8], start=(m == 0), stop=False)
                    nc.tensor.matmul(out, vs_new[:, (4 + h) * P:(5 + h) * P], ptb_new[1][:, 32 * h:32 * h + 8], start=False, stop=True)
                for h in range(MEM_H):
                    for m in range(2):
                        mm = nc.tensor.matmul(OB[:, 96 + 8 * h:104 + 8 * h], vs_mem[:, m, h * P:(h + 1) * P],
                                              ptb[2][:, m, 32 * h:32 * h + 8], start=(m == 0), stop=(m == 1))
                mm.then_inc(bo_ready, 1)
                part(1, b + J_G0, h_hi, h_lo, TOK, PART_C)

            with pe.Fori(0, KB // 2) as k:
                for br in range(2):
                    for u in range(2):
                        part(u, k * 3 + (J_MRG + br), h_hi, h_lo, TOK, ALL)
                pe.wait_ge(oz_lo_rdy, HEADS + 2)
                for u in range(2):
                    banks = ((S0, S1, S2), (P0, P1, OB))[u]
                    j = k * 3 + (J_MRG + 2)
                    part(u, j, oz_hi, oz_lo, TOK, range(0, 8), banks[0], 0, 7)
                    part(u, j, oz_hi, oz_lo, TOK, range(8, 12), banks[1], 8, 11)
                    part(u, j, oz_hi, oz_lo, TOK, range(12, 16), banks[2], 12, 15)

            pe.wait_ge(mrg_lo_rdy, KB + 1)
            with pe.Fori(0, KB // 2) as k:
                for u in range(2):
                    part(u, k + J_OUT, mrg_hi, mrg_lo, TOK, ALL)
            pe.wait_ge(y_sums, 2 * KB + 1)
            nc.tensor.matmul(S0[:, 0:TOK], ones[:], y_ss[:], start=True, stop=True).then_inc(y_ssd, 1)


def kernel(**inputs):
    import concourse.bacc as bacc
    from concourse.bass_utils import run_bass_kernel_spmd

    a = {k: np.asarray(v) for k, v in inputs.items()}
    n_pool = a["cache_sel_kv"].shape[1]

    def tiles(m, c0, n):
        return m[:, c0:c0 + n * P].reshape(KB, P, n, P).transpose(2, 1, 0, 3).reshape(n, P, KB * P)

    w_in = a["w_in"][0]
    w_br = np.concatenate([a["w_br_nsa"][0], a["w_br_moba"][0], a["w_br_mem"][0]], 0)
    sel, win, mob = tiles(w_in, W_SEL, 4), tiles(w_in, W_WIN, 4), tiles(w_in, W_KB, 8)
    g = tiles(w_in, W_GM, 48)
    br = tiles(w_br, 0, KB)
    merge = [x for k in range(KB // 2) for x in (g[16 + 2 * k:18 + 2 * k], g[32 + 2 * k:34 + 2 * k], br[2 * k:2 * k + 2])]
    stream = np.concatenate([
        tiles(a["w_mem_kv"][0], 0, 8), tiles(w_in, W_GN, 1), tiles(w_in, W_GN, 1), tiles(w_in, W_CMP, 4),
        tiles(w_in, 0, 8), tiles(w_in, W_QB, 4), tiles(w_in, W_QM, 4),
        sel[:2], win[:2], mob[:4], sel[2:], win[2:], mob[4:],
        tiles(w_in, W_ZN, 8), tiles(w_in, W_ZB, 4), tiles(w_in, W_ZM, 4), g[:16], *merge, tiles(a["w_out"][0], 0, KB)], 0)
    assert stream.shape[0] == 2 * J_END

    def blocks_t(x):
        return x.reshape(-1, KB, P).transpose(2, 1, 0)

    def keys_t(x):
        return x.transpose(0, 3, 2, 1)

    q, s = np.arange(SEQ)[:, None], np.arange(SEQ)[None, :]
    dist = np.where(s <= q, s - q, NEG).astype(np.float32)
    dist = np.concatenate([dist[:P, P:], dist[:P, :P], dist[P:]], 1)
    ends = np.arange(N_CMP) * CMP_STRIDE + CMP_LEN - 1
    seen = ends[None, :] <= np.arange(SEQ)[:, None]
    mask_cmp = np.zeros((P, 2, CMP_STRIDE), np.float32)
    mask_cmp[:, :, :N_CMP] = np.where(seen, 0.0, NEG).reshape(2, P, N_CMP).transpose(1, 0, 2)
    vis = np.repeat(seen.any(1).astype(np.float32).reshape(2, P).T[:, :, None], NSA_H, 2)
    s_nsa = 2.0 ** (-8.0 * np.arange(1, NSA_H + 1) / NSA_H)
    s_moba = 2.0 ** (-8.0 * np.arange(1, MOBA_H + 1) / MOBA_H)
    slopes = np.tile(np.concatenate([s_nsa, s_moba, np.zeros(4)]).astype(np.float32), (P, 1))
    t, s = np.arange(DEC_SEQ)[:, None] + PAST, np.arange(KEYS_S)[None, :]
    d_smp = np.where(s <= t, s - t, NEG)
    bias_nsa = np.tile((s_nsa[:, None, None] * d_smp).reshape(64, KEYS_S), (2, 1)).astype(np.float32)
    bias_moba = np.zeros((MOBA_H, 32, KEYS_S), np.float32)
    bias_moba[:, :DEC_SEQ] = s_moba[:, None, None] * d_smp

    cmp_c, sel_c, moba_c = a["cache_cmp_kv"][0], a["cache_sel_kv"][0], a["cache_moba_kv"][0]
    win_c, mem_c = a["cache_win_kv"][0], a["cache_mem_kv"][0]
    x = np.concatenate([a["x_prompt"].reshape(SEQ, D_MODEL), a["x_sample"].reshape(N_SMP, D_MODEL)], 0)
    host = {
        "stream": stream,
        "x_t": blocks_t(x),
        "m_t": blocks_t(a["mem_prompt"].reshape(N_MEM, D_MODEL)),
        "gains": np.stack([a["norm_g"][0], a["mem_norm_g"][0], a["final_norm_g"]]).reshape(3, KB, P).transpose(2, 0, 1),
        "page_table": a["page_table"].reshape(1, -1),
        "phi_w1": a["phi_w1"][0].transpose(0, 2, 1, 3),
        "phi_w2": a["phi_w2"][0].transpose(1, 0, 2),
        "phi_pos": a["phi_pos"][0].transpose(2, 0, 1),
        "cmp_pages": cmp_c.transpose(0, 2, 4, 3, 1),
        "sel_k": keys_t(sel_c[:, :, 0]), "sel_v": sel_c[:, :, 1].reshape(n_pool, PAGE, -1),
        "moba_k": keys_t(moba_c[:, :, 0]), "moba_v": moba_c[:, :, 1].reshape(n_pool, PAGE, -1),
        "win_k": keys_t(win_c[:, :, 0]), "win_v": win_c[:, :, 1].reshape(DEC_BATCH, 2, P, -1),
        "mem_k": keys_t(mem_c[:, :, 0]), "mem_v": mem_c[:, :, 1].reshape(DEC_BATCH, 2, P, -1),
        "cache_win": win_c.reshape(DEC_BATCH, PAST, -1),
        "dist": dist, "mask_cmp": mask_cmp, "vis_cmp": vis, "slopes": slopes,
        "bias_nsa": bias_nsa, "bias_moba": bias_moba.reshape(P, KEYS_S), "ident": np.eye(P, dtype=np.float32),
    }
    out_shapes = {"y_out": (KB, P, TOK), "kv_out": (20, P, TOK), "mem_out": (8, P, N_MEM), "win_old": (DEC_BATCH, PAST, 4 * HD)}

    nc = bacc.Bacc("TRN2", target_bir_lowering=False, num_devices=1)
    A, arrays = {"n_pool": n_pool}, {}
    for name, v in host.items():
        arrays["in_" + name] = np.ascontiguousarray(v)
        A[name] = nc.dram_tensor("in_" + name, v.shape, mybir.dt.from_np(v.dtype), kind="ExternalInput").ap()
    for name, shape in out_shapes.items():
        A[name] = nc.dram_tensor("out_" + name, shape, f32, kind="ExternalOutput").ap()
    build(nc, A)
    res = run_bass_kernel_spmd(nc, [arrays], core_ids=[0]).results[0]

    y = res["out_y_out"].reshape(D_MODEL, TOK).T
    kv = res["out_kv_out"].transpose(2, 0, 1)
    mem = res["out_mem_out"].transpose(2, 0, 1)

    def pick(ks, vs):
        both = np.stack([kv[:, ks], kv[:, vs]], 1)
        return both[:SEQ][None, None], both[SEQ:].reshape(1, DEC_BATCH, DEC_SEQ, 2, -1, HD)

    cmp_p, cmp_s = pick([0, 1], [2, 3])
    sel_p, sel_s = pick([4, 5], [12, 13])
    win_p, win_s = pick([6, 7], [14, 15])
    mob_p, mob_s = pick([8, 9, 10, 11], [16, 17, 18, 19])
    win_all = np.concatenate([res["out_win_old"].reshape(1, DEC_BATCH, PAST, 2, GROUPS, HD), win_s], 2)
    out = (y[:SEQ].reshape(1, SEQ, D_MODEL), y[SEQ:].reshape(DEC_BATCH, DEC_SEQ, D_MODEL),
           cmp_p, sel_p, mob_p, win_p, np.stack([mem[:, :4], mem[:, 4:]], 1)[None, None],
           cmp_s, sel_s, mob_s, win_all)
    return tuple(np.ascontiguousarray(v) for v in out)
```
